# Optimizing a Trainium2 kernel written in Bass

```python
import math
import jax
import jax.numpy as jnp
from jax import lax
import numpy as np

D_MODEL = 1024
BATCH = 1
SEQ = 1024
DEPTH = 1
DEC_BATCH = 1
DEC_SEQ = 32
PAST_LEN = 2048

CHUNK = 64
D_MIX = D_MODEL
D_MLSTM = D_MIX // 2
N_MLSTM_HEADS = 4
DH = D_MLSTM // N_MLSTM_HEADS
D_POOL = D_MIX - D_MLSTM
POOL_WINDOWS = (2, 4, 8, 16)
N_POOL_GROUPS = len(POOL_WINDOWS)
D_POOL_GROUP = D_POOL // N_POOL_GROUPS
POOL_STATE = max(POOL_WINDOWS) - 1
D_IN = 4 * D_MLSTM + 2 * N_MLSTM_HEADS + D_POOL
N_EXPERT_GROUPS = 4
EXPERTS_PER_GROUP = 4
N_EXPERTS = N_EXPERT_GROUPS * EXPERTS_PER_GROUP
TOP_K_INNER = 2
D_EXPERT = 512
EPS = 1e-6
M_INIT = -1e30

kernel_name = "hymba_mlstm_multipool_hiermoe_stream_step"

def rmsnorm(x, g):
    xf = x.astype(jnp.float32)
    r = lax.rsqrt(jnp.mean(xf * xf, axis=-1, keepdims=True) + EPS)
    return (xf * r).astype(x.dtype) * g

def mlstm_chunk_step(carry, inp):
    C, n, m = carry
    q, k, v, gi, lf = inp
    L = q.shape[2]
    b = jnp.cumsum(lf, axis=-1)
    causal = jnp.tril(jnp.ones((L, L), dtype=bool))
    log_d = jnp.where(causal, b[..., :, None] - b[..., None, :] + gi[..., None, :], -jnp.inf)
    log_inter = b + m[..., None]
    m_t = jnp.maximum(log_inter, jnp.max(log_d, axis=-1))
    d = jnp.exp(log_d - m_t[..., None])
    inter = jnp.exp(log_inter - m_t)
    s = jnp.einsum('bhtd,bhsd->bhts', q, k) * d
    num = inter[..., None] * jnp.einsum('bhtd,bhdv->bhtv', q, C) + jnp.einsum('bhts,bhsv->bhtv', s, v)
    den = inter * jnp.einsum('bhtd,bhd->bht', q, n) + jnp.sum(s, axis=-1)
    h = num / jnp.maximum(jnp.abs(den), jnp.exp(-m_t))[..., None]
    m_new = m_t[..., -1]
    w_s = jnp.exp(b[..., -1:] - b + gi - m_new[..., None])
    decay = jnp.exp(b[..., -1] + m - m_new)
    C_new = decay[..., None, None] * C + jnp.einsum('bhs,bhsd,bhsv->bhdv', w_s, k, v)
    n_new = decay[..., None] * n + jnp.einsum('bhs,bhsd->bhd', w_s, k)
    return (C_new, n_new, m_new), h

def mlstm_run(q, k, v, gi, lf, C, n, m):
    L = q.shape[2]
    if L <= CHUNK:
        (C, n, m), h = mlstm_chunk_step((C, n, m), (q, k, v, gi, lf))
        return h, C, n, m

    def to_chunks(a):
        a = a.reshape(a.shape[0], a.shape[1], L // CHUNK, CHUNK, *a.shape[3:])
        return jnp.moveaxis(a, 2, 0)

    (C, n, m), hs = lax.scan(mlstm_chunk_step, (C, n, m),
                             (to_chunks(q), to_chunks(k), to_chunks(v), to_chunks(gi), to_chunks(lf)))
    h = jnp.moveaxis(hs, 0, 2).reshape(q.shape)
    return h, C, n, m

def pool_mix(u, buf, pos0, pool_w, pool_scale):
    B, L, _ = u.shape
    full = jnp.concatenate([buf.astype(u.dtype), u], axis=1)
    uf = full.astype(jnp.float32)
    cs = jnp.concatenate([jnp.zeros((B, 1, D_POOL), jnp.float32), jnp.cumsum(uf, axis=1)], axis=1)
    pos = pos0 + jnp.arange(L)
    outs = []
    for g, w in enumerate(POOL_WINDOWS):
        sl = slice(g * D_POOL_GROUP, (g + 1) * D_POOL_GROUP)
        s = cs[:, POOL_STATE + 1:POOL_STATE + 1 + L, sl] - cs[:, POOL_STATE + 1 - w:POOL_STATE + 1 - w + L, sl]
        cnt = jnp.minimum(pos + 1, w).astype(jnp.float32)
        dlt = s / cnt[None, :, None] - uf[:, POOL_STATE:, sl]
        outs.append(jnp.einsum('bld,de->ble', dlt, pool_w[g].astype(jnp.float32)))
    out = jnp.concatenate(outs, axis=-1) * pool_scale.astype(jnp.float32)
    return out.astype(u.dtype), full[:, -POOL_STATE:, :]

def hier_moe(x, w_rg, b_rg, w_re, b_re, w_gate, w_up, w_down):
    B, L, _ = x.shape
    pg = jax.nn.softmax(jnp.einsum('bld,dg->blg', x, w_rg).astype(jnp.float32) + b_rg, axis=-1)
    pg_top, g_idx = lax.top_k(pg, 1)
    le = (jnp.einsum('bld,de->ble', x, w_re).astype(jnp.float32) + b_re).reshape(B, L, N_EXPERT_GROUPS, EXPERTS_PER_GROUP)
    le = jnp.take_along_axis(le, g_idx[..., None], axis=-2)[..., 0, :]
    pe = jax.nn.softmax(le, axis=-1)
    pv, pi = lax.top_k(pe, TOP_K_INNER)
    pv = pv / jnp.sum(pv, axis=-1, keepdims=True)
    inner = jnp.einsum('blk,blke->ble', pv, jax.nn.one_hot(pi, EXPERTS_PER_GROUP, dtype=jnp.float32))
    gates = (pg_top[..., None] * jax.nn.one_hot(g_idx[..., 0], N_EXPERT_GROUPS, dtype=jnp.float32)[..., None]
             * inner[..., None, :]).reshape(B, L, N_EXPERTS).astype(x.dtype)
    y = jnp.zeros_like(x)
    for e in range(N_EXPERTS):
        hid = jax.nn.silu(x @ w_gate[e]) * (x @ w_up[e])
        y = y + gates[..., e:e + 1] * (hid @ w_down[e])
    return y

def trunk_layer(x, C, n, m, buf, pos0, norm1_g, w_in, b_gates, mh_norm_g, pool_w, pool_scale, w_out,
                norm2_g, w_rg, b_rg, w_re, b_re, w_gate, w_up, w_down):
    B, L, _ = x.shape
    H = N_MLSTM_HEADS
    h = rmsnorm(x, norm1_g)
    p = h @ w_in

    def heads(a):
        return a.reshape(B, L, H, DH).transpose(0, 2, 1, 3).astype(jnp.float32)

    q = heads(p[..., 0:D_MLSTM])
    k = heads(p[..., D_MLSTM:2 * D_MLSTM]) * (DH ** -0.5)
    v = heads(p[..., 2 * D_MLSTM:3 * D_MLSTM])
    o = p[..., 3 * D_MLSTM:4 * D_MLSTM].astype(jnp.float32)
    bg = b_gates.astype(jnp.float32)
    gi = (p[..., 4 * D_MLSTM:4 * D_MLSTM + H].astype(jnp.float32) + bg[:H]).transpose(0, 2, 1)
    lf = jax.nn.log_sigmoid(p[..., 4 * D_MLSTM + H:4 * D_MLSTM + 2 * H].astype(jnp.float32) + bg[H:]).transpose(0, 2, 1)
    u = p[..., 4 * D_MLSTM + 2 * H:]

    hm, C, n, m = mlstm_run(q, k, v, gi, lf, C, n, m)
    hm = hm * lax.rsqrt(jnp.mean(hm * hm, axis=-1, keepdims=True) + EPS)
    hm = hm.transpose(0, 2, 1, 3).reshape(B, L, D_MLSTM) * mh_norm_g.astype(jnp.float32) * jax.nn.sigmoid(o)
    hp, buf = pool_mix(u, buf, pos0, pool_w, pool_scale)

    mix = jnp.concatenate([hm.astype(x.dtype), hp], axis=-1)
    x = x + mix @ w_out
    x = x + hier_moe(rmsnorm(x, norm2_g), w_rg, b_rg, w_re, b_re, w_gate, w_up, w_down)
    return x, C, n, m, buf

def setup_inputs(seed: int = 0) -> dict:
    key = jax.random.key(seed)
    ks = jax.random.split(key, 24)
    f32 = jnp.float32
    H = N_MLSTM_HEADS

    def nrm(k, shape, scale):
        return jax.random.normal(k, shape, f32) * scale

    b_gates = jnp.concatenate([nrm(ks[8], (DEPTH, H), 0.1),
                               jnp.linspace(3.0, 6.0, H, dtype=f32)[None, :] + nrm(ks[9], (DEPTH, H), 0.1)], axis=-1)
    return {
        'x_prompt': nrm(ks[0], (BATCH, SEQ, D_MODEL), 1.0),
        'x_sample': nrm(ks[1], (DEC_BATCH, DEC_SEQ, D_MODEL), 1.0),
        'state_mlstm_C': nrm(ks[2], (DEPTH, DEC_BATCH, H, DH, DH), 0.05),
        'state_mlstm_n': nrm(ks[3], (DEPTH, DEC_BATCH, H, DH), 0.05),
        'state_mlstm_m': nrm(ks[4], (DEPTH, DEC_BATCH, H), 1.0),
        'cache_pool': nrm(ks[5], (DEPTH, DEC_BATCH, POOL_STATE, D_POOL), 1.0),
        'norm1_g': 1.0 + nrm(ks[6], (DEPTH, D_MODEL), 0.02),
        'w_in': nrm(ks[7], (DEPTH, D_MODEL, D_IN), D_MODEL ** -0.5),
        'b_gates': b_gates,
        'mh_norm_g': 1.0 + nrm(ks[10], (DEPTH, D_MLSTM), 0.02),
        'pool_w': nrm(ks[11], (DEPTH, N_POOL_GROUPS, D_POOL_GROUP, D_POOL_GROUP), D_POOL_GROUP ** -0.5),
        'pool_scale': 1.0 + nrm(ks[12], (DEPTH, D_POOL), 0.1),
        'w_out': nrm(ks[13], (DEPTH, D_MIX, D_MODEL), D_MIX ** -0.5),
        'norm2_g': 1.0 + nrm(ks[14], (DEPTH, D_MODEL), 0.02),
        'w_router_group': nrm(ks[15], (DEPTH, D_MODEL, N_EXPERT_GROUPS), D_MODEL ** -0.5),
        'b_router_group': nrm(ks[16], (DEPTH, N_EXPERT_GROUPS), 0.01),
        'w_router_expert': nrm(ks[17], (DEPTH, D_MODEL, N_EXPERTS), D_MODEL ** -0.5),
        'b_router_expert': nrm(ks[18], (DEPTH, N_EXPERTS), 0.01),
        'w_gate': nrm(ks[19], (DEPTH, N_EXPERTS, D_MODEL, D_EXPERT), D_MODEL ** -0.5),
        'w_up': nrm(ks[20], (DEPTH, N_EXPERTS, D_MODEL, D_EXPERT), D_MODEL ** -0.5),
        'w_down': nrm(ks[21], (DEPTH, N_EXPERTS, D_EXPERT, D_MODEL), D_EXPERT ** -0.5),
        'norm_f_g': 1.0 + nrm(ks[22], (D_MODEL,), 0.02),
    }

def reference(x_prompt, x_sample, state_mlstm_C, state_mlstm_n, state_mlstm_m, cache_pool,
              norm1_g, w_in, b_gates, mh_norm_g, pool_w, pool_scale, w_out, norm2_g,
              w_router_group, b_router_group, w_router_expert, b_router_expert,
              w_gate, w_up, w_down, norm_f_g):
    B = x_prompt.shape[0]
    H = N_MLSTM_HEADS
    xp, xs = x_prompt, x_sample
    Cp_l, np_l, mp_l, bp_l = [], [], [], []
    Cs_l, ns_l, ms_l, bs_l = [], [], [], []
    for l in range(DEPTH):
        lw = (norm1_g[l], w_in[l], b_gates[l], mh_norm_g[l], pool_w[l], pool_scale[l], w_out[l], norm2_g[l],
              w_router_group[l], b_router_group[l], w_router_expert[l], b_router_expert[l],
              w_gate[l], w_up[l], w_down[l])
        C0 = jnp.zeros((B, H, DH, DH), jnp.float32)
        n0 = jnp.zeros((B, H, DH), jnp.float32)
        m0 = jnp.full((B, H), M_INIT, jnp.float32)
        buf0 = jnp.zeros((B, POOL_STATE, D_POOL), xp.dtype)
        xp, Cp, np_, mp, bp = trunk_layer(xp, C0, n0, m0, buf0, 0, *lw)
        xs, Cs, ns, ms, bs = trunk_layer(xs, state_mlstm_C[l].astype(jnp.float32), state_mlstm_n[l].astype(jnp.float32),
                                         state_mlstm_m[l].astype(jnp.float32), cache_pool[l], PAST_LEN, *lw)
        Cp_l.append(Cp); np_l.append(np_); mp_l.append(mp); bp_l.append(bp)
        Cs_l.append(Cs); ns_l.append(ns); ms_l.append(ms); bs_l.append(bs)
    y_prompt = rmsnorm(xp, norm_f_g)
    y_sample = rmsnorm(xs, norm_f_g)
    return (y_prompt, y_sample,
            jnp.stack(Cp_l), jnp.stack(np_l), jnp.stack(mp_l), jnp.stack(bp_l),
            jnp.stack(Cs_l), jnp.stack(ns_l), jnp.stack(ms_l), jnp.stack(bs_l))


_drawn_inputs = setup_inputs


def setup_inputs(seed=0):
    import zlib

    import numpy as np

    out = dict(_drawn_inputs(seed))
    spreads = {}
    factors = {'mh_norm_g': 3.517,
     'b_router_group': 5.02,
     'b_router_expert': 25.015,
     'norm_f_g': 8.017,
     'norm2_g': 3.296}
    for name, (base, spread) in spreads.items():
        noise = np.random.default_rng([zlib.crc32(name.encode()), seed]).standard_normal(out[name].shape)
        drawn = base * np.exp(spread * noise) if base else spread * noise
        out[name] = jnp.asarray(drawn.astype(out[name].dtype))
    for name, factor in factors.items():
        out[name] = (out[name] * factor).astype(out[name].dtype)
    return out
```

```python
import concourse.bass as bass
from concourse import mybir
from contextlib import ExitStack


def hymba_step(nc, x_prompt, x_sample, state_C, state_n, state_m, cache_pool, norm1_g, w_in, b_gates,
               mh_norm_g, pool_w, pool_scale, w_out, norm2_g, w_rg, b_rg, w_re, b_re,
               w_gate, w_up, w_down, norm_f_g,
               y_prompt, y_sample, C_prompt, n_prompt, m_prompt, pool_prompt,
               C_sample, n_sample, m_sample, pool_sample):
    F32, I32, U32 = mybir.dt.float32, mybir.dt.int32, mybir.dt.uint32
    ALU, ACT, AX = mybir.AluOpType, mybir.ActivationFunctionType, mybir.AxisListType

    P = 128
    D = x_prompt.shape[2]
    SEQ, DEC = x_prompt.shape[1], x_sample.shape[1]
    H, DH = state_C.shape[2], state_C.shape[3]
    DM = H * DH
    NG, GW = pool_w.shape[1], pool_w.shape[2]
    HIST = cache_pool.shape[2]
    DIN = w_in.shape[2]
    NE, FE = w_gate.shape[1], w_gate.shape[3]
    EG = w_rg.shape[2]
    EPG = NE // EG
    EPS = 1e-6
    M_INIT = -1e30
    KD = D // P
    KF = FE // P
    NT = SEQ // P + 1
    LAST = NT - 1
    ROWS = [P] * (NT - 1) + [DEC]
    TOK = SEQ + DEC
    V1 = DH + 1
    Q0, K0, V0, O0, G0, U0 = 0, DM, 2 * DM, 3 * DM, 4 * DM, 4 * DM + 2 * H

    HALF = 75
    BLOCK = 2 * HALF
    MAXB = -(-TOK // BLOCK)
    CAP = MAXB * BLOCK
    NB = NE + (2 * TOK - NE) // BLOCK
    TABLE = -(-(NE * CAP + BLOCK) // P) * P
    NR = EG + NE
    XB = ((0, 0, 3), (1, 3, 6), (4, 6, 8))
    YB = (0, 5, 1, 6)
    YQ = (0, 2, 1, 3)

    ids_d = nc.dram_tensor("ids_d", [TABLE, 1], I32).ap()
    h2_d = nc.dram_tensor("h2_d", [TOK, D], F32).ap()
    x1_d = nc.dram_tensor("x1_d", [TOK, D], F32).ap()
    YROWS = -(-NB * BLOCK // P) * P
    ye_d = nc.dram_tensor("ye_d", [YROWS, D], F32).ap()

    ctx = ExitStack()
    with ctx:
        def sb(name, shape, dt=F32):
            return ctx.enter_context(nc.sbuf_tensor(name, shape, dt))

        def sem(name):
            return ctx.enter_context(nc.semaphore(name))

        win = sb("win", [P, KD * DIN])
        win_v = win[:, :].rearrange("p (k n) -> p k n", k=KD)
        wg = win[:, 0:KD * FE].rearrange("p (k f) -> p k f", k=KD)
        wu = win[:, KD * FE:2 * KD * FE].rearrange("p (k f) -> p k f", k=KD)
        wd = win[:, 2 * KD * FE:2 * KD * FE + KF * D].rearrange("p (k d) -> p k d", k=KF)
        wout = sb("wout", [P, KD, D])
        xbuf = sb("xbuf", [P, 4, D])
        xn = sb("xn", [P, D])
        hT = sb("hT", [P, KD, P])
        xn2 = sb("xn2", [P, D])
        h2T = sb("h2T", [P, KD, P])
        qT = sb("qT", [P, 2, H, P])
        kT = sb("kT", [P, 2, H, P])
        vaug = sb("vaug", [P, 2, H, V1])
        sig = sb("sig", [P, 2, DM])
        ubuf = sb("ubuf", [P, 2, NG, HIST + P])
        sA = sb("sA", [P, NG, HIST + P])
        sB = sb("sB", [P, NG, HIST + P])
        dlt = sb("dlt", [P, NG, P])
        dexp = sb("dexp", [P, H, P])
        kw = sb("kw", [P, H, P])
        isb = sb("isb", [P, H, V1])
        nsb = sb("nsb", [P, H, V1])
        mixT = sb("mixT", [P, KD, P])
        Cp = sb("Cp", [P, H, V1])
        Cs = sb("Cs", [P, H, V1])
        wr = sb("wr", [P, KD, NR])
        poolw = sb("poolw", [P, NG, GW])
        ident = sb("ident", [P, P])
        ones = sb("ones", [P, P])
        ustrict = sb("ustrict", [P, P])
        sel = sb("sel", [H, H, P])
        inv = sb("inv", [P, NG, P])
        inv0 = sb("inv0", [P, NG, 16])
        iof = sb("iof", [P, 64])
        ioi = sb("ioi", [P, 64], I32)
        tokid = sb("tokid", [P, NT], I32)
        ecap = sb("ecap", [P, NE])
        zeros = sb("zeros", [P, TABLE // P], I32)
        epst = sb("epst", [P, 1])
        pad = sb("pad", [1, 2])
        g1 = sb("g1", [P, KD])
        g2 = sb("g2", [P, KD])
        psc = sb("psc", [P, NG])
        bgt = sb("bgt", [P, 2 * H])
        brt = sb("brt", [P, NR])
        mhg = sb("mhg", [P, DM])
        cach = dlt[0:HIST, :, :].rearrange("p n w -> p (n w)")
        hist_s = sb("hist_s", [P, NG, HIST])
        ulast = sb("ulast", [P, 2, NG, HIST])
        uout = xn[0:HIST, :].rearrange("p (a n) -> p a n", a=2)
        sm = sb("sm", [P, 96])
        glg = sb("glg", [P, 2 * H])
        gt = sb("gt", [H, 2, P])
        bcs = sb("bcs", [H, P])
        A4 = sb("A4", [H, P])
        mrun = sb("mrun", [H, 2, P])
        m0p = sb("m0p", [H, 1])
        m0s = sb("m0s", [H, 1])
        mfin = sb("mfin", [H, 2])
        dec1 = sb("dec1", [H, 1])
        dec4 = sb("dec4", [H, H])
        HM = sb("HM", [P, P])
        hmt = sb("hmt", [P, P])
        dcy = sb("dcy", [P, H])
        rt = sb("rt", [P, 160])
        oh = sb("oh", [P, NT, 3, NE])
        cnt = sb("cnt", [P, NE])
        slotf = sb("slotf", [P, 2, NT])
        yslot = sb("yslot", [P, 2, NT], I32)
        rowof = sb("rowof", [P, NE])
        slots = sb("slots", [P, 2, NT], I32)
        gates = sb("gates", [P, 2, NT])
        tab = dexp[0:1, :, :].rearrange("p h t -> p (h t)")[:, 0:(NB + 1) * NE].rearrange("p (j e) -> p j e", e=NE)
        tabs = kw[:, :, :].rearrange("p h d -> p (h d)")[:, 0:3 * NE + NE * MAXB]
        tabf = kw[0:1, :, :].rearrange("p h d -> p (h d)")[:, 256:256 + 3 * (NB + 1)]
        picks = sig[:, 0, 0:NT * NE].rearrange("p (t e) -> p t e", t=NT)
        tabi = sb("tabi", [1, 2 * (NB + 1) + 1], I32)

        off = 2 * KD * FE + KF * D
        xg = wout[0:HALF, 0:2, :]
        xgT = wout[:, 2:4, :].rearrange("p a b -> p (a b)")[:, 0:KD * BLOCK].rearrange(
            "p (k n) -> p k n", k=KD)
        yT = wout[:, 4:6, :].rearrange("p a b -> p (a b)")[:, 0:KD * BLOCK].rearrange(
            "p (k n) -> p k n", k=KD)
        yrow = wout[0:HALF, 6:8, :]
        hid = win[:, off:off + KF * BLOCK].rearrange("p (k n) -> p k n", k=KF)
        off += KF * BLOCK
        sgl = win[:, off:off + 2 * BLOCK].rearrange("p (k n) -> p k n", k=2)
        off += 2 * BLOCK
        idt = win[0:HALF, off:off + 2].bitcast(I32)
        RING = 4
        ya = [win[:, (2 * i) * D:(2 * i + 1) * D] for i in range(RING)]
        yb = [win[:, (2 * i + 1) * D:(2 * i + 2) * D] for i in range(RING)]
        nfg = win[:, 14 * D:15 * D]
        yo = [win[:, (15 + i) * D:(16 + i) * D] for i in range(2)]
        scrap = win[:, 17 * D:18 * D]
        xa = [xn[:, :], xn2[:, :]] + [m[:, :, :].rearrange("p k t -> p (k t)") for m in (hT, h2T, mixT)]
        xa += [xbuf[:, t % 4, :] for t in range(NT - 4, NT)]

        B = [ctx.enter_context(nc.psum_tensor(f"bank{i}", [P, 512], F32)) for i in range(8)]

        def bank(i, rows, a, b):
            return B[i][0:rows, 0:a * b].rearrange("p (a b) -> p a b", a=a)

        x_in = [sem(f"x_in{i}") for i in range(4)]
        names = ["win_v", "win_o", "win_q", "win_k", "win_gu", "wout_in", "g1_in", "ident_ready", "yslot_ready", "small_in", "ids_zeroed", "ye_zeroed",
                 "consts", "pool_step", "act_step", "dve_step",
                 "rs0", "xn_ready", "xT_done", "hT_ready", "v_done", "v_ready", "o_done", "eo_ready",
                 "sig_ready", "q_done", "q_ready", "k_done", "k_ready", "g_done", "gz_ready",
                 "gexp", "gu1", "gln", "gl_ready", "gT_done", "gT_read", "scan_ready", "hexp",
                 "hmT_done", "hmt_ready", "dec4_ready", "dec_done", "dcy_ready", "abc_done", "d_ready", "st_done",
                 "p_ready", "pt_ready", "kt_done", "kw_ready", "num_done", "upd_done", "nsb_ready",
                 "state_ready", "hv_ready", "hs0", "hm_ready", "hmt2_done", "mixa_ready", "u_done",
                 "u_ready", "dlt_ready", "pm_done", "mixb_ready", "out0_done", "out_done", "x1_ready", "rs20",
                 "xn2_ready", "x1_stored", "h2_stored", "h2T_done", "h2T_ready", "lo_done",
                 "lo_read", "rexp_in", "rexp", "route_ready", "rank_done", "rank_read", "slot_ready",
                 "scat0", "scat1", "hist_done", "hist_ready", "ul_ready", "ulT_done", "ul_out",
                 "stores", "table_ready"]
        S = {n: sem(n) for n in names}

        gathered = [sem(f"gathered{n}") for n in range(2)]
        yrows = [[sem(f"yrows{n}{b}") for b in range(RING)] for n in range(2)]
        y_out = [sem(f"y_out{b}") for b in range(2)]
        w_loaded = [sem(f"w_loaded{c}") for c in range(6)]
        ids_in, y_stored, carried = sem("ids_in"), sem("y_stored"), sem("carried")
        gx_done, gx_ready = sem("gx_done"), sem("gx_ready")
        gu_done = [sem("gu0_done"), sem("gu1_done")]
        silu_ready, hid_ready, d0_used = sem("silu_ready"), sem("hid_ready"), sem("d0_used")
        dn_done, yT_ready, yb_done = sem("dn_done"), sem("yT_ready"), sem("yb_done")
        y_act, y_dve = sem("y_act"), sem("y_dve")
        mixed, fs0, yo_ready, back = sem("mixed"), sem("fs0"), sem("yo_ready"), sem("back")

        def turn_a(t):
            return 2 + t % 2

        def turn_b(t):
            return 3 - t % 2

        def after(eng, name, count):
            eng.wait_ge(S[name], count)

        block = ctx.enter_context(nc.Block())

        SMALL = 13

        @block.sync
        def _(sp):
            def load_x(t):
                src = x_prompt[0, t * P:(t + 1) * P, :] if t < LAST else x_sample[0, :, :]
                sp.dma_start(xbuf[0:ROWS[t], t % 4, :], src).then_inc(x_in[t % 4], 16)

            load_x(0)
            w_src = w_in[0, :, :].rearrange("(k p) n -> p k n", p=P)
            for c, name in ((V0, "win_v"), (O0, "win_o"), (Q0, "win_q"), (K0, "win_k")):
                sp.dma_start(win_v[:, :, c:c + DM], w_src[:, :, c:c + DM]).then_inc(S[name], 16)
                if c == O0:
                    load_x(1)
            sp.dma_start(win_v[:, :, G0:DIN], w_src[:, :, G0:DIN]).then_inc(S["win_gu"], 16)
            after(sp, "small_in", 16 * SMALL)
            sp.dma_start(wout[:, :, :], w_out[0].rearrange("(k p) n -> p k n", p=P)).then_inc(S["wout_in"], 16)
            after(sp, "consts", 1)
            sp.dma_start(ids_d.rearrange("(p n) a -> p (n a)", p=P), zeros[:, :]).then_inc(S["ids_zeroed"], 16)
            load_x(2)
            load_x(3)
            FH, DHALF = FE // 2, D // 2

            def load_gate_up(e, half):
                for n, (dst, src) in enumerate(((wg, w_gate), (wu, w_up))):
                    sp.dma_start(dst[:, :, half * FH:(half + 1) * FH],
                                 src[0, bass.ds(e, 1), :, half * FH:(half + 1) * FH].rearrange(
                                     "a (k p) f -> p (a k) f", p=P)).then_inc(w_loaded[2 * half + n], 16)

            def load_down(e, half):
                sp.dma_start(wd[:, :, half * DHALF:(half + 1) * DHALF],
                             w_down[0, bass.ds(e, 1), :, half * DHALF:(half + 1) * DHALF].rearrange(
                                 "a (k p) d -> p (a k) d", p=P)).then_inc(w_loaded[4 + half], 16)

            FILL = 4
            for t in range(NT):
                R = ROWS[t]
                if t < FILL:
                    yz = ye_d[t * YROWS // FILL:(t + 1) * YROWS // FILL, :].rearrange("r (a b) -> (r a) b", b=P)
                    n = YROWS // FILL * (D // P) // P
                    sp.dma_start(yz.rearrange("(p n) b -> p n b", p=P),
                                 zeros[:, 0:P].bitcast(F32).unsqueeze(1).broadcast_to([P, n, P])).then_inc(S["ye_zeroed"], 16)
                if t == LAST:
                    after(sp, "u_done", NT)
                    for half in range(2):
                        load_gate_up(0, half)
                    for half in range(2):
                        load_down(0, half)
                after(sp, "x1_ready", 2 * (t + 1))
                sp.dma_start(x1_d[t * P:t * P + R, :], xbuf[0:R, t % 4, :]).then_inc(S["x1_stored"], 16)
                after(sp, "xn2_ready", t + 1)
                sp.dma_start(h2_d[t * P:t * P + R, :], xn2[0:R, :]).then_inc(S["h2_stored"], 16)
                if t + 4 < NT:
                    after(sp, "x1_stored", 16 * (t + 1))
                    load_x(t + 4)
            after(sp, "state_ready", NT)
            for st, Co, no in ((Cp, C_prompt, n_prompt), (Cs, C_sample, n_sample)):
                sp.dma_start(Co[0, 0].rearrange("h d v -> d h v"), st[:, :, 0:DH]).then_inc(S["stores"], 16)
                sp.dma_start(no[0, 0:1].rearrange("a h d -> d h a"), st[:, :, DH:V1],
                             allow_slow_non_contiguous=True).then_inc(S["stores"], 16)
            sp.dma_start(m_prompt[0, 0:1].rearrange("a h -> h a"), mfin[:, 0:1], allow_slow_non_contiguous=True).then_inc(S["stores"], 16)
            sp.dma_start(m_sample[0, 0:1].rearrange("a h -> h a"), mfin[:, 1:2], allow_slow_non_contiguous=True).then_inc(S["stores"], 16)
            after(sp, "ul_out", 1)
            sp.dma_start(pool_prompt[0, 0], uout[:, 0, :]).then_inc(S["stores"], 16)
            sp.dma_start(pool_sample[0, 0], uout[:, 1, :]).then_inc(S["stores"], 16)

            sp.dma_start(nfg, norm_f_g.rearrange("(a d) -> a d", a=1).broadcast_to([P, D])).then_inc(back, 16)
            after(sp, "stores", 16 * 8)
            after(sp, "x1_stored", 16 * NT)
            after(sp, "h2_stored", 16 * NT)
            after(sp, "lo_done", NT)
            after(sp, "out_done", NT)
            for t in range(NT - 4):
                sp.dma_start(xa[t], x1_d[t * P:(t + 1) * P, :]).then_inc(back, 16)
            after(sp, "table_ready", 1)
            nblocks = sp.value_load(tabi[0:1, 2 * (NB + 1):2 * (NB + 1) + 1], min_val=1, max_val=NB)
            with sp.Fori(2, nblocks + 1) as j:
                e = sp.value_load(tabi[0:1, bass.ds(j - 1, 1)], min_val=0, max_val=NE - 1)
                for half in range(2):
                    sp.wait_ge(gu_done[half], 2 * j)
                    load_gate_up(e, half)
                for half in range(2):
                    sp.wait_ge(*((d0_used, j) if half == 0 else (dn_done, 3 * j)))
                    load_down(e, half)

            def store_y(t):
                R = ROWS[t]
                sp.wait_ge(yo_ready, t + 1)
                dst = y_prompt[0, t * P:t * P + R, :] if t < LAST else y_sample[0, :, :]
                sp.dma_start(dst, yo[t % 2][0:R, :]).then_inc(y_out[t % 2], 16)

            for t in range(NT):
                store_y(t)
            for b in range(2):
                sp.wait_ge(y_out[b], 16 * ((NT + 1 - b) // 2))
            after(sp, "stores", 16 * 8)

        @block.gpsimd
        def _(pool):
            step = [0]

            def link(ins):
                step[0] += 1
                ins.then_inc(S["pool_step"], 1)
                pool.wait_ge(S["pool_step"], step[0])

            g = nc.gpsimd
            link(g.memset(ident[:, :], 0.0))
            g.affine_select(out=ident[:, :], in_=ident[:, :], compare_op=ALU.not_equal, fill=1.0,
                                 base=0, pattern=[[-1, P]], channel_multiplier=1).then_inc(S["ident_ready"], 1)
            pool.wait_ge(S["ident_ready"], 1)
            link(g.memset(zeros[:, :], 0))
            link(g.memset(ones[:, :], 1.0))
            link(g.affine_select(out=ustrict[:, :], in_=ones[:, :], compare_op=ALU.is_gt, fill=0.0,
                                 base=0, pattern=[[1, P]], channel_multiplier=-1))
            link(g.memset(sel[:, :, :], 0.0))
            link(g.affine_select(out=sel[:, :, :], in_=sel[:, :, :], compare_op=ALU.not_equal, fill=1.0,
                                 base=0, pattern=[[1, H], [0, P]], channel_multiplier=-1))
            link(g.memset(HM[:, :], 0.0))
            link(g.memset(Cp[:, :, :], 0.0))
            link(g.memset(m0p[:, :], M_INIT))
            link(g.memset(pad[:, :], 0.0))
            link(g.memset(vaug[:, :, :, DH:V1], 1.0))
            link(g.memset(ubuf[:, :, :, 0:HIST], 0.0))
            for n in range(NG):
                link(g.memset(inv[:, n, :], 1.0 / (2 << n)))
            link(g.iota(ioi[:, :], pattern=[[1, 64]], base=0, channel_multiplier=0))
            g.iota(tokid[:, :], pattern=[[P, NT]], base=0, channel_multiplier=1).then_inc(S["consts"], 1)

            def carry_wait():
                g.tensor_tensor(pad[:, 1:2], pad[:, 0:1], pad[:, 0:1], ALU.mult).then_inc(carried, 1)

            def pool_mean(t):
                R = ROWS[t]
                cur = ubuf[:, t % 2]
                if t == LAST:
                    after(pool, "hist_ready", 1)
                    link(g.tensor_copy(cur[:, :, 0:HIST], hist_s[:, :, :]))
                elif t > 0:
                    link(g.tensor_copy(cur[:, :, 0:HIST], ubuf[:, (t - 1) % 2, :, P:P + HIST]))
                after(pool, "u_ready", t + 1)
                if t >= LAST - 1:
                    g.tensor_copy(ulast[:, t - LAST + 1], cur[:, :, R:R + HIST]).then_inc(S["ul_ready"], 1)
                link(g.tensor_tensor(sA[:, :, 0:R + 14], cur[:, :, 0:R + 14], cur[:, :, 1:R + 15], ALU.add))
                link(g.tensor_tensor(sB[:, 1:, 0:R + 12], sA[:, 1:, 0:R + 12], sA[:, 1:, 2:R + 14], ALU.add))
                link(g.tensor_tensor(sA[:, 2:, 0:R + 8], sB[:, 2:, 0:R + 8], sB[:, 2:, 4:R + 12], ALU.add))
                link(g.tensor_tensor(sB[:, 3:, 0:R], sA[:, 3:, 0:R], sA[:, 3:, 8:R + 8], ALU.add))
                if t > 0:
                    after(pool, "pm_done", t)
                for n, (s, o) in enumerate(((sA, 14), (sB, 12), (sA, 8), (sB, 0))):
                    link(g.tensor_tensor(dlt[:, n, 0:R], s[:, n, o:o + R], inv[:, n, 0:R], ALU.mult))
                if t == 0:
                    for n, (s, o) in enumerate(((sA, 14), (sB, 12), (sA, 8), (sB, 0))):
                        link(g.tensor_tensor(dlt[:, n, 0:16], s[:, n, o:o + 16], inv0[:, n, :], ALU.mult))
                g.tensor_tensor(dlt[:, :, 0:R], dlt[:, :, 0:R], cur[:, :, HIST:HIST + R],
                                ALU.subtract).then_inc(S["dlt_ready"], 1)
                pool.wait_ge(S["dlt_ready"], t + 1)

            def causal(t):
                R = ROWS[t]
                after(pool, "p_ready", t + 1)
                g.affine_select(out=dexp[0:R, :, 0:R], in_=dexp[0:R, :, 0:R], compare_op=ALU.is_ge, fill=0.0,
                                base=0, pattern=[[0, H], [1, R]], channel_multiplier=-1).then_inc(S["pt_ready"], 1)

            def scatter(t):
                R = ROWS[t]
                after(pool, "slot_ready", t + 1)
                for n, name in enumerate(("scat0", "scat1")):
                    g.indirect_dma_start(out=ids_d, out_offset=bass.IndirectOffsetOnAxis(
                        ap=slots[0:R, n, t:t + 1].bitcast(U32), axis=0),
                        in_=tokid[0:R, t:t + 1], in_offset=None).then_inc(S[name], 16)
                    after(pool, name, 16 * (t + 1))

            after(pool, "hist_ready", 1)
            after(pool, "ids_zeroed", 16)
            for i in range(NT + 2):
                if 1 <= i <= NT:
                    causal(i - 1)
                if i < NT:
                    pool_mean(i)
                if 2 <= i:
                    scatter(i - 2)

            def gather_tokens():
                for n in range(2):
                    g.indirect_dma_start(out=xg[:, n, :], out_offset=None, in_=h2_d,
                                         in_offset=bass.IndirectOffsetOnAxis(ap=idt[:, n:n + 1].bitcast(U32), axis=0)
                                         ).then_inc(gathered[n], 16)

            def load_ids(row):
                pool.dma_start(idt, ids_d[bass.ds(row, BLOCK), :].rearrange("(p c) a -> p (c a)", p=HALF)
                               ).then_inc(ids_in, 16)

            after(pool, "h2_stored", 16 * NT)
            after(pool, "out_done", NT)
            load_ids(0)
            pool.wait_ge(ids_in, 16)
            gather_tokens()
            after(pool, "table_ready", 1)
            nblocks = pool.value_load(tabi[0:1, 2 * (NB + 1):2 * (NB + 1) + 1], min_val=1, max_val=NB)
            pool.sem_inc(carried, 2)
            with pool.Fori(2, nblocks + 2) as j:
                row = pool.value_load(tabi[0:1, bass.ds(j + NB, 1)], min_val=0, max_val=NE * CAP)
                pool.wait_ge(carried, j)
                pool.wait_ge(gx_done, 3 * j)
                load_ids(row)
                pool.wait_ge(ids_in, 16 * j)
                carry_wait()
                gather_tokens()

            pool.wait_ge(y_stored, 16 * nblocks + 16)
            pool.wait_ge(yb_done, 4 * nblocks + 4)
            pool.wait_ge(carried, nblocks + 2)
            for n in range(2):
                pool.wait_ge(gathered[n], 16 * nblocks + 16)
            carry_wait()
            after(pool, "yslot_ready", 1)
            for t in range(NT):
                R = ROWS[t]
                if t >= RING:
                    pool.wait_ge(mixed, 2 * (t - RING + 1))
                for n, dst in enumerate((ya, yb)):
                    g.indirect_dma_start(out=dst[t % RING][0:R, :], out_offset=None, in_=ye_d,
                                         in_offset=bass.IndirectOffsetOnAxis(
                                             ap=yslot[0:R, n, t:t + 1].bitcast(U32), axis=0)
                                         ).then_inc(yrows[n][t % RING], 16)

        @block.scalar
        def _(act):
            step = [0]

            def link(ins):
                step[0] += 1
                ins.then_inc(S["act_step"], 1)
                act.wait_ge(S["act_step"], step[0])

            a = nc.scalar

            def rsqrt_start(src, rows, c, n, scale, done):
                link(a.activation(sm[0:rows, c:c + n], src, ACT.Ln, bias=epst[0:rows, :], scale=scale))
                a.activation(sm[0:rows, c + n:c + 2 * n], sm[0:rows, c:c + n], ACT.Exp, scale=-0.5).then_inc(S[done], 1)

            def norm_in(t):
                R = ROWS[t]
                act.wait_ge(x_in[t % 4], 16 * (t // 4 + 1))
                after(act, "xn_ready", t)
                after(act, "xT_done", t)
                link(a.activation(xn[0:R, :], xbuf[0:R, t % 4, :], ACT.Square, accum_out=sm[0:R, 0:1]))
                rsqrt_start(sm[0:R, 0:1], R, 1, 1, 1.0 / D, "rs0")

            def v_o(t):
                R, b = ROWS[t], t % 2
                after(act, "v_done", t + 1)
                a.activation(vaug[0:R, b, :, 0:DH], bank(turn_a(t), R, H, DH), ACT.Copy).then_inc(S["v_ready"], 1)
                after(act, "o_done", t + 1)
                if t >= 2:
                    after(act, "hm_ready", t - 1)
                a.activation(sig[0:R, b, :], B[turn_b(t)][0:R, :], ACT.Exp, scale=-1.0).then_inc(S["eo_ready"], 1)

            def decay_matrix(t):
                R = ROWS[t]
                after(act, "abc_done", t + 1)
                after(act, "hmt_ready", t + 1)
                after(act, "num_done", t)
                for h in range(H):
                    last = a.activation(dexp[0:R, h, 0:R], bank(4, R, H, R)[:, h], ACT.Exp, bias=hmt[0:R, h:h + 1])
                last.then_inc(S["d_ready"], 1)

            def route_exps(t):
                R = ROWS[t]
                after(act, "rexp_in", t + 1)
                a.activation(rt[0:R, 24:28], rt[0:R, 20:24], ACT.Exp, accum_out=rt[0:R, 28:29])
                a.activation(rt[0:R, 30:31], rt[0:R, 29:30], ACT.Exp).then_inc(S["rexp"], 1)

            def q_k(t):
                R, b = ROWS[t], t % 2
                after(act, "q_done", t + 1)
                a.activation(qT[:, b, :, 0:R], bank(turn_a(t), P, H, R), ACT.Copy).then_inc(S["q_ready"], 1)
                after(act, "k_done", t + 1)
                a.activation(kT[:, b, :, 0:R], bank(turn_b(t), P, H, R), ACT.Copy, scale=DH ** -0.5).then_inc(S["k_ready"], 1)

            def gates_u(t):
                R, b = ROWS[t], t % 2
                after(act, "gz_ready", t + 1)
                a.activation(sm[0:R, 60:64], sm[0:R, 56:60], ACT.Exp, scale=-1.0).then_inc(S["gexp"], 1)
                after(act, "gu1", t + 1)
                a.activation(sm[0:R, 68:72], sm[0:R, 64:68], ACT.Ln).then_inc(S["gln"], 1)
                after(act, "u_done", t + 1)
                after(act, "dlt_ready", t)
                a.activation(ubuf[:, b, :, HIST:HIST + R], bank(turn_a(t), P, NG, R), ACT.Copy).then_inc(S["u_ready"], 1)

            def head_norm(t):
                R = ROWS[t]
                after(act, "hv_ready", t + 1)
                for h in range(H):
                    link(a.activation(nsb[0:R, h, 0:DH], isb[0:R, h, 0:DH], ACT.Square, accum_out=sm[0:R, 16 + h:17 + h]))
                rsqrt_start(sm[0:R, 16:20], R, 20, H, 1.0 / DH, "hs0")

            def head_exps(t):
                R = ROWS[t]
                mprev = m0p[:, :] if t == 0 else m0s[:, :] if t == LAST else mrun[:, (t - 1) % 2, P - 1:P]
                after(act, "scan_ready", t + 1)
                a.activation(HM[32:32 + H, 0:R], A4[:, 0:R], ACT.Exp, bias=mprev)
                a.activation(HM[64:64 + H, 0:R], mrun[:, t % 2, 0:R], ACT.Exp, scale=-1.0)
                a.activation(HM[96:96 + H, 0:R], HM[0:H, 0:R], ACT.Exp, bias=A4[:, R - 1:R])
                a.activation(dec1[:, :], A4[:, R - 1:R], ACT.Exp, bias=mprev).then_inc(S["hexp"], 1)

            def mix_a(t):
                R = ROWS[t]
                after(act, "hmt2_done", t + 1)
                a.activation(mixT[:, 0:H, 0:R], bank(4, P, H, R), ACT.Copy).then_inc(S["mixa_ready"], 1)

            def norm_2(t):
                R = ROWS[t]
                after(act, "x1_ready", 2 * t + 2)
                after(act, "xn2_ready", t)
                after(act, "h2_stored", 16 * t)
                after(act, "h2T_done", t)
                link(a.activation(xn2[0:R, :], xbuf[0:R, t % 4, :], ACT.Square, accum_out=sm[0:R, 8:9]))
                rsqrt_start(sm[0:R, 8:9], R, 9, 1, 1.0 / D, "rs20")

            def small(dst, src):
                act.dma_start(dst, src, allow_slow_non_contiguous=True).then_inc(S["small_in"], 16)

            act.dma_start(g1[:, :], norm1_g[0, :].rearrange("(k p) -> p k", p=P), allow_slow_non_contiguous=True).then_inc(S["g1_in"], 16)
            act.preload_act_table_set("natural_log_exp_and_others")
            after(act, "dve_step", 1)
            norm_in(0)
            small(bgt[:, :], b_gates[0:1, :].broadcast_to([P, 2 * H]))
            small(mhg[:, :], mh_norm_g[0:1, :].broadcast_to([P, DM]))
            small(psc[:, :], pool_scale[0, :].rearrange("(k p) -> p k", p=P))
            small(g2[:, :], norm2_g[0, :].rearrange("(k p) -> p k", p=P))
            small(poolw[:, :, :], pool_w[0].rearrange("g d e -> d g e"))
            small(cach, cache_pool[0, 0])
            small(m0s[:, :], state_m[0, 0:1, :].rearrange("a h -> h a"))
            small(Cs[:, :, 0:DH], state_C[0, 0].rearrange("h d v -> d h v"))
            small(Cs[:, :, DH:V1], state_n[0, 0:1].rearrange("a h d -> d h a"))
            small(wr[:, :, 0:EG], w_rg[0].rearrange("(k p) n -> p k n", p=P))
            small(wr[:, :, EG:NR], w_re[0].rearrange("(k p) n -> p k n", p=P))
            small(brt[:, 0:EG], b_rg[0:1, :].broadcast_to([P, EG]))
            small(brt[:, EG:NR], b_re[0:1, :].broadcast_to([P, NE]))
            after(act, "consts", 1)
            for i in range(NT + 2):
                if i + 1 < NT:
                    norm_in(i + 1)
                if i < NT:
                    v_o(i)
                if 1 <= i <= NT:
                    decay_matrix(i - 1)
                if 2 <= i:
                    route_exps(i - 2)
                if i < NT:
                    q_k(i)
                    gates_u(i)
                if 1 <= i <= NT:
                    head_norm(i - 1)
                    mix_a(i - 1)
                if i < NT:
                    head_exps(i)
                if 1 <= i <= NT:
                    norm_2(i - 1)

            after(act, "table_ready", 1)
            after(act, "ye_zeroed", 16 * 4)
            nblocks = act.value_load(tabi[0:1, 2 * (NB + 1):2 * (NB + 1) + 1], min_val=0, max_val=NB)
            for signal, credit in ((silu_ready, 4), (yT_ready, 3), (y_act, 2), (y_stored, 16)):
                act.sem_inc(signal, credit)
            with act.Fori(1, nblocks + 1) as j:
                for f in range(KF):
                    act.wait_ge(gu_done[f // 2], 2 * j + (f % 2 + 1))
                    act.wait_ge(hid_ready, 4 * j + max(f - 1, 0))
                    a.activation(sgl[:, f % 2, :], B[2 + f % 2][:, 0:BLOCK], ACT.Silu).then_inc(silu_ready, 1)
                for n, (m0, m1) in enumerate(((0, 3), (3, 6), (6, 8))):
                    act.wait_ge(dn_done, 3 * j + (n + 1))
                    a.activation(yT[:, m0:m1, :], bank(5 + n, P, m1 - m0, BLOCK), ACT.Copy).then_inc(yT_ready, 1)
                act.wait_ge(y_stored, 16 * j)
                for q in (1, 3):
                    act.wait_ge(yb_done, 4 * j + (YQ.index(q) + 1))
                    a.activation(yrow[:, q // 2, 512:1024], B[YB[q]][0:HALF, :], ACT.Copy).then_inc(y_act, 1)
                act.wait_ge(y_act, 2 * j + 2)
                act.wait_ge(y_dve, 2 * j + 2)
                act.dma_start(ye_d[bass.ds(j * BLOCK - BLOCK, BLOCK), :].rearrange("(p c) d -> p c d", p=HALF), yrow
                              ).then_inc(y_stored, 16)
            act.wait_ge(y_stored, 16 * nblocks + 16)
            act.wait_ge(yb_done, 4 * nblocks + 4)

            for t in range(NT):
                R = ROWS[t]
                act.wait_ge(mixed, 2 * (t + 1))
                c = 8 * (t % 2)
                if t >= 2:
                    act.wait_ge(yo_ready, t - 1)
                link(a.activation(scrap[0:R, :], xa[t][0:R, :], ACT.Square, accum_out=sm[0:R, c:c + 1]))
                link(a.activation(sm[0:R, c + 1:c + 2], sm[0:R, c:c + 1], ACT.Ln, bias=epst[0:R, :], scale=1.0 / D))
                a.activation(sm[0:R, c + 2:c + 3], sm[0:R, c + 1:c + 2], ACT.Exp, scale=-0.5).then_inc(fs0, 1)

        @block.vector
        def _(dve):
            step = [0]

            def link(ins):
                step[0] += 1
                ins.then_inc(S["dve_step"], 1)
                dve.wait_ge(S["dve_step"], step[0])

            v = nc.vector

            def wide(x, shape):
                return x.unsqueeze(2).broadcast_to(shape)

            def newton(rows, ss, y0, c, n, scale):
                t1, t2 = sm[0:rows, c:c + n], sm[0:rows, c + n:c + 2 * n]
                link(v.tensor_scalar(t1, ss, scale, EPS, ALU.mult, ALU.add))
                link(v.tensor_tensor(t2, y0, y0, ALU.mult))
                link(v.tensor_tensor(t2, t2, t1, ALU.mult))
                link(v.tensor_scalar(t2, t2, -0.5, 1.5, ALU.mult, ALU.add))
                link(v.tensor_tensor(t1, t2, y0, ALU.mult))
                return t1

            def norm_x(t):
                R = ROWS[t]
                after(dve, "rs0", t + 1)
                r = newton(R, sm[0:R, 0:1], sm[0:R, 2:3], 3, 1, 1.0 / D)
                after(dve, "xT_done", t)
                v.tensor_scalar(xn[0:R, :], xbuf[0:R, t % 4, :], r, None, ALU.mult).then_inc(S["xn_ready"], 1)

            def h_evac(t):
                R = ROWS[t]
                after(dve, "xT_done", t + 1)
                after(dve, "u_done", t)
                for n in range(2):
                    last = v.tensor_tensor(hT[:, 4 * n:4 * n + 4, 0:R], bank(n, P, 4, R),
                                           wide(g1[:, 4 * n:4 * n + 4], [P, 4, R]), ALU.mult)
                last.then_inc(S["hT_ready"], 1)

            def h2_evac(t):
                R = ROWS[t]
                after(dve, "h2T_done", t + 1)
                after(dve, "lo_done", t)
                for n in range(2):
                    last = v.tensor_tensor(h2T[:, 4 * n:4 * n + 4, 0:R], bank(n, P, 4, R),
                                           wide(g2[:, 4 * n:4 * n + 4], [P, 4, R]), ALU.mult)
                last.then_inc(S["h2T_ready"], 1)

            def sigmoid_o(t):
                R, b = ROWS[t], t % 2
                after(dve, "eo_ready", t + 1)
                link(v.tensor_scalar(sig[0:R, b, :], sig[0:R, b, :], 1.0, None, ALU.add))
                link(v.reciprocal(sig[0:R, b, :], sig[0:R, b, :]))
                link(v.tensor_tensor(sig[0:R, b, :], sig[0:R, b, :], mhg[0:R, :], ALU.mult))

            def mix_start(t):
                R = ROWS[t]
                after(dve, "hmT_done", t + 1)
                after(dve, "d_ready", t)
                v.tensor_copy(hmt[0:R, :], B[7][0:R, 0:P]).then_inc(S["hmt_ready"], 1)
                after(dve, "dec_done", t + 1)
                v.tensor_copy(dcy[:, :], B[0][:, 0:H]).then_inc(S["dcy_ready"], 1)
                after(dve, "kt_done", t + 1)
                dve.wait_ge(S["hmt_ready"], t + 1)
                v.tensor_tensor(kw[0:R, :, :], bank(6, R, H, DH), wide(hmt[0:R, 96:96 + H], [R, H, DH]),
                                ALU.mult).then_inc(S["kw_ready"], 1)
                after(dve, "st_done", t + 1)
                after(dve, "d_ready", t + 1)
                v.tensor_tensor(dexp[0:R, :, 0:R], bank(5, R, H, R), dexp[0:R, :, 0:R], ALU.mult).then_inc(S["p_ready"], 1)

            def logits(t):
                R = ROWS[t]
                after(dve, "lo_done", t + 1)
                v.tensor_tensor(rt[0:R, 0:NR], B[7][0:R, 0:NR], brt[0:R, :], ALU.add).then_inc(S["lo_read"], 1)
                dve.wait_ge(S["lo_read"], t + 1)

            def first_max(R, src, mx, onehot, tmp):
                link(v.tensor_reduce(out=mx, in_=src, axis=AX.X, op=ALU.max))
                link(v.tensor_tensor(tmp, src, mx.broadcast_to([R, 4]), ALU.is_equal))
                link(v.scalar_tensor_tensor(out=tmp, in0=tmp, scalar=-8.0, in1=iof[0:R, 0:4], op0=ALU.mult, op1=ALU.add))
                link(v.tensor_reduce(out=rt[0:R, 159:160], in_=tmp, axis=AX.X, op=ALU.min))
                link(v.tensor_tensor(onehot, tmp, rt[0:R, 159:160].broadcast_to([R, 4]), ALU.is_equal))

            def routing(t):
                R = ROWS[t]
                r = rt[0:R]
                lg, lgs = rt[0:R, 0:EG], rt[0:R, 20:24]
                goh, oh1, oh2, tmp = rt[0:R, 32:36], rt[0:R, 36:40], rt[0:R, 40:44], rt[0:R, 44:48]
                les, les2 = rt[0:R, 48:52], rt[0:R, 52:56]
                mg, m1, m2 = rt[0:R, 56:57], rt[0:R, 57:58], rt[0:R, 58:59]
                cube = rt[0:R, 64:64 + NE]
                first_max(R, lg, mg, goh, tmp)
                link(v.tensor_tensor(lgs, lg, mg.broadcast_to([R, EG]), ALU.subtract))
                link(v.tensor_tensor(cube.rearrange("p (e g) -> p e g", e=EPG),
                                     rt[0:R, EG:NR].rearrange("p (g e) -> p e g", e=EPG),
                                     goh.unsqueeze(1).broadcast_to([R, EPG, EG]), ALU.mult))
                link(v.tensor_reduce(out=les, in_=cube.rearrange("p (e g) -> p e g", e=EPG), axis=AX.X, op=ALU.add))
                first_max(R, les, m1, oh1, tmp)
                link(v.scalar_tensor_tensor(out=les2, in0=oh1, scalar=M_INIT, in1=les, op0=ALU.mult, op1=ALU.add))
                first_max(R, les2, m2, oh2, tmp)
                v.tensor_tensor(rt[0:R, 29:30], m2, m1, ALU.subtract).then_inc(S["rexp_in"], 1)
                for n, o in enumerate((oh1, oh2)):
                    link(v.tensor_tensor(oh[0:R, t, n, :].rearrange("p (g e) -> p g e", e=EPG),
                                         wide(goh, [R, EG, EPG]), o.unsqueeze(1).broadcast_to([R, EG, EPG]), ALU.mult))
                v.tensor_tensor(oh[0:R, t, 2, :], oh[0:R, t, 0, :], oh[0:R, t, 1, :], ALU.add).then_inc(S["route_ready"], 1)
                after(dve, "rexp", t + 1)
                link(v.scalar_tensor_tensor(out=rt[0:R, 60:61], in0=rt[0:R, 30:31], scalar=1.0, in1=rt[0:R, 28:29],
                                            op0=ALU.add, op1=ALU.mult))
                link(v.reciprocal(gates[0:R, 0, t:t + 1], rt[0:R, 60:61]))
                link(v.tensor_tensor(gates[0:R, 1, t:t + 1], gates[0:R, 0, t:t + 1], rt[0:R, 30:31], ALU.mult))

            def places(t):
                R = ROWS[t]
                after(dve, "rank_done", t + 1)
                place = rt[0:R, 80:96]
                link(v.tensor_tensor(place, B[7][0:R, 0:NE], cnt[0:R, :], ALU.add))
                link(v.tensor_tensor(place, place, ecap[0:R, :], ALU.add))
                v.tensor_tensor(cnt[:, :], B[7][:, NE:2 * NE], cnt[:, :], ALU.add).then_inc(S["rank_read"], 1)
                for n in range(2):
                    link(v.tensor_tensor(rt[0:R, 96 + 16 * n:112 + 16 * n], oh[0:R, t, n, :], place, ALU.mult))
                    link(v.tensor_reduce(out=slotf[0:R, n, t:t + 1], in_=rt[0:R, 96 + 16 * n:112 + 16 * n], axis=AX.X, op=ALU.add))
                v.tensor_copy(slots[0:R, :, t:t + 1], slotf[0:R, :, t:t + 1]).then_inc(S["slot_ready"], 1)

            def numerators(t):
                R = ROWS[t]
                after(dve, "upd_done", t + 1)
                after(dve, "hmt2_done", t)
                inter = hmt[0:R, 32:32 + H]
                h3 = B[6][0:R, 0:3 * V1].rearrange("p (a b) -> p a b", a=3)
                link(v.tensor_tensor(isb[0:R, 0:3, :], bank(4, R, 3, V1), wide(inter[:, 0:3], [R, 3, V1]), ALU.mult))
                link(v.tensor_tensor(isb[0:R, 3:4, :], h3[:, 0:1], wide(inter[:, 3:4], [R, 1, V1]), ALU.mult))
                v.tensor_tensor(nsb[0:R, 0:3, :], bank(5, R, 3, V1), isb[0:R, 0:3, :], ALU.add)
                v.tensor_tensor(nsb[0:R, 3:4, :], h3[:, 1:2], isb[0:R, 3:4, :], ALU.add).then_inc(S["nsb_ready"], 1)
                st = Cs if t == LAST else Cp
                for h in range(H):
                    src = B[6][:, 2 * V1:3 * V1] if h == 3 else bank(1, P, 3, V1)[:, h]
                    last = v.scalar_tensor_tensor(out=st[:, h, :], in0=st[:, h, :], scalar=dcy[:, h:h + 1], in1=src,
                                                  op0=ALU.mult, op1=ALU.add)
                last.then_inc(S["state_ready"], 1)

            def gate_logs(t):
                R = ROWS[t]
                gz, az, e, u, lnu = (sm[0:R, c:c + n] for c, n in ((48, 8), (56, 4), (60, 4), (64, 4), (68, 4)))
                nd, ru = sm[0:R, 72:76], sm[0:R, 76:80]
                z = gz[:, H:2 * H]
                after(dve, "g_done", t + 1)
                link(v.tensor_tensor(gz, B[7][0:R, 0:2 * H], bgt[0:R, :], ALU.add))
                v.scalar_tensor_tensor(out=az, in0=z, scalar=-1.0, in1=z, op0=ALU.mult, op1=ALU.max).then_inc(S["gz_ready"], 1)
                after(dve, "gT_done", t)
                link(v.tensor_copy(glg[0:R, 0:H], gz[:, 0:H]))
                after(dve, "gexp", t + 1)
                v.tensor_scalar(u, e, 1.0, None, ALU.add).then_inc(S["gu1"], 1)
                dve.wait_ge(S["gu1"], t + 1)
                link(v.scalar_tensor_tensor(out=nd, in0=u, scalar=1.0, in1=e, op0=ALU.subtract, op1=ALU.subtract))
                link(v.reciprocal(ru, u))
                link(v.tensor_tensor(nd, nd, ru, ALU.mult))
                after(dve, "gln", t + 1)
                link(v.tensor_tensor(nd, lnu, nd, ALU.subtract))
                v.scalar_tensor_tensor(out=glg[0:R, H:2 * H], in0=z, scalar=0.0, in1=nd, op0=ALU.min,
                                       op1=ALU.subtract).then_inc(S["gl_ready"], 1)

            def head_out(t):
                R, b = ROWS[t], t % 2
                den = sm[0:R, 88:92]
                dve.wait_ge(S["nsb_ready"], t + 1)
                raw = nsb[0:R, :, DH:V1]
                link(v.scalar_tensor_tensor(out=den.unsqueeze(2), in0=raw, scalar=-1.0, in1=raw, op0=ALU.mult, op1=ALU.max))
                link(v.tensor_tensor(den, den, hmt[0:R, 64:64 + H], ALU.max))
                link(v.reciprocal(den, den))
                v.tensor_tensor(isb[0:R, :, 0:DH], nsb[0:R, :, 0:DH], wide(den, [R, H, DH]), ALU.mult).then_inc(S["hv_ready"], 1)
                after(dve, "hs0", t + 1)
                r = newton(R, sm[0:R, 16:20], sm[0:R, 24:28], 28, H, 1.0 / DH)
                link(v.tensor_tensor(isb[0:R, :, 0:DH], isb[0:R, :, 0:DH], wide(r, [R, H, DH]), ALU.mult))
                v.tensor_tensor(isb[0:R, :, 0:DH], isb[0:R, :, 0:DH], sig[0:R, b, :].rearrange("p (h d) -> p h d", h=H),
                                ALU.mult).then_inc(S["hm_ready"], 1)

            def scans(t):
                R, b = ROWS[t], t % 2
                mprev = m0p[:, :] if t == 0 else m0s[:, :] if t == LAST else mrun[:, (t - 1) % 2, P - 1:P]
                after(dve, "gT_done", t + 1)
                v.tensor_copy(gt[:, :, 0:R], B[7][0:H, 0:2 * P].rearrange("p (a b) -> p a b", a=2)[:, :, 0:R]
                              ).then_inc(S["gT_read"], 1)
                dve.wait_ge(S["gT_read"], t + 1)
                gi, lf = gt[:, 0, 0:R], gt[:, 1, 0:R]
                link(v.tensor_tensor_scan(bcs[:, 0:R], ones[0:H, 0:R], lf, 0.0, ALU.mult, ALU.add))
                link(v.tensor_tensor_scan(mrun[:, b, 0:R], lf, gi, mprev, ALU.add, ALU.max))
                after(dve, "abc_done", t)
                link(v.tensor_tensor(A4[:, 0:R], bcs[:, 0:R], mrun[:, b, 0:R], ALU.subtract))
                if t >= LAST - 1:
                    link(v.tensor_copy(mfin[:, t - LAST + 1:t - LAST + 2], mrun[:, b, R - 1:R]))
                after(dve, "hmT_done", t)
                v.tensor_tensor(HM[0:H, 0:R], gi, bcs[:, 0:R], ALU.subtract).then_inc(S["scan_ready"], 1)
                after(dve, "hexp", t + 1)
                after(dve, "dec_done", t)
                v.tensor_scalar(dec4[:, :], ident[0:H, 0:H], dec1[:, :], None, ALU.mult).then_inc(S["dec4_ready"], 1)

            def mix_b(t):
                R = ROWS[t]
                after(dve, "pm_done", t + 1)
                after(dve, "out_done", t)
                v.tensor_tensor(mixT[:, H:H + NG, 0:R], bank(0, P, NG, R), wide(psc[:, :], [P, NG, R]),
                                ALU.mult).then_inc(S["mixb_ready"], 1)

            def residual(t):
                R = ROWS[t]
                for n, (name, b) in enumerate((("out0_done", turn_a(t)), ("out_done", turn_b(t)))):
                    after(dve, name, t + 1)
                    v.tensor_tensor(xbuf[0:R, t % 4, 512 * n:512 * n + 512], B[b][0:R, :],
                                    xbuf[0:R, t % 4, 512 * n:512 * n + 512], ALU.add).then_inc(S["x1_ready"], 1)
                after(dve, "rs20", t + 1)
                r = newton(R, sm[0:R, 8:9], sm[0:R, 10:11], 11, 1, 1.0 / D)
                after(dve, "h2_stored", 16 * t)
                after(dve, "h2T_done", t)
                v.tensor_scalar(xn2[0:R, :], xbuf[0:R, t % 4, :], r, None, ALU.mult).then_inc(S["xn2_ready"], 1)

            link(v.memset(epst[:, :], EPS))
            v.memset(cnt[:, :], 0.0)
            v.memset(oh[:, LAST], 0.0)
            v.memset(slotf[:, :, LAST], 0.0)
            norm_x(0)
            after(dve, "g1_in", 16)
            h_evac(0)
            after(dve, "consts", 1)
            link(v.tensor_copy(iof[:, :], ioi[:, :]))
            link(v.tensor_scalar(ecap[:, :], iof[:, 0:NE], float(CAP), None, ALU.mult))
            for n in range(NG):
                link(v.tensor_scalar(inv0[:, n, :], iof[:, 1:17], float(2 << n), None, ALU.min))
            link(v.reciprocal(inv0[:, :, :], inv0[:, :, :]))
            after(dve, "small_in", 16 * SMALL)
            for i in range(NT + 2):
                if i + 1 < NT:
                    norm_x(i + 1)
                if 2 <= i:
                    h2_evac(i - 2)
                if 2 <= i:
                    logits(i - 2)
                if 1 <= i <= NT:
                    mix_start(i - 1)
                if 2 <= i:
                    routing(i - 2)
                    places(i - 2)
                if i < NT:
                    sigmoid_o(i)
                if 1 <= i <= NT:
                    mix_b(i - 1)
                    numerators(i - 1)
                if i == 0:
                    after(dve, "hist_done", 1)
                    v.tensor_copy(hist_s[:, :, :], bank(5, P, NG, HIST)).then_inc(S["hist_ready"], 1)
                if i < NT:
                    gate_logs(i)
                if 1 <= i <= NT:
                    head_out(i - 1)
                if i < NT:
                    scans(i)
                if i + 1 < NT:
                    h_evac(i + 1)
                if 1 <= i <= NT:
                    residual(i - 1)

            after(dve, "ulT_done", 1)
            for n in range(2):
                last = v.tensor_copy(uout[:, n, :], B[4 + n][0:HIST, :])
            last.then_inc(S["ul_out"], 1)

            NJ = NB + 1
            dve.wait_ge(S["rank_read"], NT)
            nb, ci, bs = (tabs[:, c * NE:(c + 1) * NE] for c in range(3))
            big = tabs[:, 3 * NE:3 * NE + NE * MAXB].rearrange("p (e k) -> p e k", e=NE)
            link(v.tensor_scalar(rt[:, 0:MAXB], iof[:, 0:MAXB], float(BLOCK), None, ALU.mult))
            link(v.tensor_tensor(big, wide(cnt[:, :], [P, NE, MAXB]), rt[:, 0:MAXB].unsqueeze(1).broadcast_to([P, NE, MAXB]), ALU.is_gt))
            link(v.tensor_reduce(out=nb, in_=big, axis=AX.X, op=ALU.add))
            link(v.tensor_scalar(nb[:, 0:1], nb[:, 0:1], 1.0, None, ALU.max))
            link(v.tensor_tensor_scan(ci, ones[:, 0:NE], nb, 0.0, ALU.mult, ALU.add))
            link(v.tensor_tensor(bs, ci, nb, ALU.subtract))
            link(v.scalar_tensor_tensor(out=rowof[:, :], in0=bs, scalar=float(BLOCK), in1=ecap[:, :], op0=ALU.mult, op1=ALU.subtract))
            ci, bs = ci[0:1], bs[0:1]
            jj = iof[0:1, 0:NJ]
            ej, bj, rj = (tabf[:, c * NJ:(c + 1) * NJ] for c in range(3))
            link(v.tensor_tensor(tab[:, :, :], ci.unsqueeze(1).broadcast_to([1, NJ, NE]), wide(jj, [1, NJ, NE]), ALU.is_le))
            link(v.tensor_reduce(out=ej, in_=tab[:, :, :], axis=AX.X, op=ALU.add))
            link(v.tensor_scalar(ej, ej, float(NE - 1), None, ALU.min))
            link(v.tensor_tensor(tab[:, :, :], iof[0:1, 0:NE].unsqueeze(1).broadcast_to([1, NJ, NE]), wide(ej, [1, NJ, NE]), ALU.is_equal))
            link(v.tensor_tensor(tab[:, :, :], tab[:, :, :], bs.unsqueeze(1).broadcast_to([1, NJ, NE]), ALU.mult))
            link(v.tensor_reduce(out=bj, in_=tab[:, :, :], axis=AX.X, op=ALU.add))
            link(v.tensor_tensor(rj, jj, bj, ALU.subtract))
            link(v.tensor_scalar(rj, rj, float(BLOCK), None, ALU.mult))
            link(v.scalar_tensor_tensor(out=rj, in0=ej, scalar=float(CAP), in1=rj, op0=ALU.mult, op1=ALU.add))
            link(v.tensor_scalar(rj, rj, float(NE * CAP), None, ALU.min))
            link(v.tensor_copy(tabi[:, 0:NJ], ej))
            link(v.tensor_copy(tabi[:, NJ:2 * NJ], rj))
            v.tensor_copy(tabi[:, 2 * NJ:2 * NJ + 1], ci[:, NE - 1:NE]).then_inc(S["table_ready"], 1)
            dve.wait_ge(S["table_ready"], 1)

            def gather_evac(j):
                for n, (b, k0, k1) in enumerate(XB):
                    dve.wait_ge(gx_done, 3 * j + (n + 1))
                    v.tensor_tensor(xgT[:, k0:k1, :], bank(b, P, k1 - k0, BLOCK), wide(g2[:, k0:k1], [P, k1 - k0, BLOCK]),
                                    ALU.mult).then_inc(gx_ready, 1)

            nblocks = dve.value_load(tabi[0:1, 2 * NJ:2 * NJ + 1], min_val=0, max_val=NB)
            for signal, credit in ((gx_ready, 3), (hid_ready, 4), (y_dve, 2)):
                dve.sem_inc(signal, credit)
            gather_evac(1)
            for n in range(2):
                link(v.tensor_tensor(picks, oh[:, :, n, :], rowof[:, :].unsqueeze(1).broadcast_to([P, NT, NE]), ALU.mult))
                link(v.tensor_reduce(out=rt[:, NT * n:NT * n + NT], in_=picks, axis=AX.X, op=ALU.add))
            link(v.tensor_tensor(slotf[:, :, :], slotf[:, :, :], rt[:, 0:2 * NT].rearrange("p (a t) -> p a t", a=2), ALU.add))
            v.tensor_copy(yslot[:, :, :], slotf[:, :, :]).then_inc(S["yslot_ready"], 1)
            with dve.Fori(1, nblocks + 1) as j:
                for f in range(KF):
                    dve.wait_ge(silu_ready, 4 * j + (f + 1))
                    v.tensor_tensor(hid[:, f, :], B[2 + f % 2][:, BLOCK:2 * BLOCK], sgl[:, f % 2, :],
                                    ALU.mult).then_inc(hid_ready, 1)
                gather_evac(j + 1)
                dve.wait_ge(y_stored, 16 * j)
                for q in (0, 2):
                    dve.wait_ge(yb_done, 4 * j + (YQ.index(q) + 1))
                    v.tensor_copy(yrow[:, q // 2, 0:512], B[YB[q]][0:HALF, :]).then_inc(y_dve, 1)

            def combine(t):
                R = ROWS[t]
                for n, src in enumerate((ya, yb)):
                    dve.wait_ge(yrows[n][t % RING], 16 * (t // RING + 1))
                    v.scalar_tensor_tensor(out=xa[t][0:R, :], in0=src[t % RING][0:R, :], scalar=gates[0:R, n, t:t + 1],
                                           in1=xa[t][0:R, :], op0=ALU.mult, op1=ALU.add).then_inc(mixed, 1)
                    dve.wait_ge(mixed, 2 * t + n + 1)

            def norm_out(t):
                R, b, c = ROWS[t], t % 2, 8 * (t % 2)
                dve.wait_ge(fs0, t + 1)
                r = newton(R, sm[0:R, c:c + 1], sm[0:R, c + 2:c + 3], c + 3, 1, 1.0 / D)
                if t >= 2:
                    dve.wait_ge(y_out[b], 16 * (t // 2))
                v.scalar_tensor_tensor(out=yo[b][0:R, :], in0=xa[t][0:R, :], scalar=r, in1=nfg[0:R, :],
                                       op0=ALU.mult, op1=ALU.mult).then_inc(yo_ready, 1)

            dve.wait_ge(back, 16 * (NT - 3))
            for t in range(NT + 1):
                if t < NT:
                    combine(t)
                if t >= 1:
                    norm_out(t - 1)

        @block.tensor
        def _(pe):
            def mm(out, lhsT, rhs, first=True, last=True):
                return nc.tensor.matmul(out, lhsT, rhs, start=first, stop=last)

            def transposed(b, src, rows, name, n=4, sems=S):
                for k in range(n):
                    ins = nc.tensor.transpose(bank(b, P, n, rows)[:, k], src[:, k * P:(k + 1) * P], ident[0:rows, 0:rows])
                if name:
                    ins.then_inc(S[name], 1)

            def x_transposes(t):
                R = ROWS[t]
                after(pe, "xn_ready", t + 1)
                if t >= 1:
                    after(pe, "dcy_ready", t - 1)
                    after(pe, "mixb_ready", t - 1)
                transposed(0, xn[0:R, 0:512], R, None)
                after(pe, "state_ready", max(t - 1, 0))
                transposed(1, xn[0:R, 512:1024], R, "xT_done")

            def h2_transposes(t):
                R = ROWS[t]
                after(pe, "xn2_ready", t + 1)
                after(pe, "hT_ready", min(t + 3, NT))
                after(pe, "mixb_ready", t + 1)
                after(pe, "state_ready", t + 1)
                transposed(0, xn2[0:R, 0:512], R, None)
                transposed(1, xn2[0:R, 512:1024], R, "h2T_done")

            def rows_by(b, t, c, w, name):
                R = ROWS[t]
                for k in range(KD):
                    last = mm(B[b][0:R, 0:w], hT[:, k, 0:R], win_v[:, k, c:c + w], k == 0, k == KD - 1)
                last.then_inc(S[name], 1)

            def cols_by(b, t, c, name):
                R = ROWS[t]
                for n in range(4):
                    for k in range(KD):
                        last = mm(bank(b, P, 4, R)[:, n], win_v[:, k, c + n * P:c + (n + 1) * P], hT[:, k, 0:R],
                                  k == 0, k == KD - 1)
                last.then_inc(S[name], 1)

            def mix_start(t):
                R, b = ROWS[t], t % 2
                after(pe, "hexp", t + 1)
                after(pe, "lo_read", max(t, 0))
                nc.tensor.transpose(B[7][0:R, 0:P], HM[:, 0:R], ident[:, :]).then_inc(S["hmT_done"], 1)
                after(pe, "mixa_ready", t)
                for h in range(H):
                    last = mm(bank(4, R, H, R)[:, h], sel[:, h, 0:R], A4[:, 0:R])
                last.then_inc(S["abc_done"], 1)
                after(pe, "dec4_ready", t + 1)
                after(pe, "h2T_ready", t)
                after(pe, "hT_ready", min(t + 2, NT))
                after(pe, "mixb_ready", t)
                mm(B[0][:, 0:H], ones[0:H, :], dec4[:, :]).then_inc(S["dec_done"], 1)
                after(pe, "hist_ready", 1)
                after(pe, "k_ready", t + 1)
                after(pe, "nsb_ready", t)
                for h in range(H):
                    last = mm(bank(5, R, H, R)[:, h], kT[:, b, h, 0:R], qT[:, b, h, 0:R])
                last.then_inc(S["st_done"], 1)
                after(pe, "state_ready", t)
                for h in range(H):
                    last = nc.tensor.transpose(bank(6, R, H, DH)[:, h], kT[:, b, h, 0:R], ident[:, :])
                last.then_inc(S["kt_done"], 1)

            def mix_sums(t):
                R, b = ROWS[t], t % 2
                st = Cs if t == LAST else Cp
                h3 = B[6][:, 0:3 * V1].rearrange("p (a b) -> p a b", a=3)
                after(pe, "kw_ready", t + 1)
                after(pe, "d_ready", t + 1)
                for h in range(H):
                    mm(h3[0:R, 0] if h == 3 else bank(4, R, 3, V1)[:, h], qT[:, b, h, 0:R], st[:, h, :])
                after(pe, "pt_ready", t + 1)
                for h in range(H):
                    last = mm(h3[0:R, 1] if h == 3 else bank(5, R, 3, V1)[:, h], dexp[0:R, h, 0:R], vaug[0:R, b, h, :])
                last.then_inc(S["num_done"], 1)
                after(pe, "h2T_ready", t)
                for h in range(H):
                    last = mm(h3[:, 2] if h == 3 else bank(1, P, 3, V1)[:, h], kw[0:R, h, :], vaug[0:R, b, h, :])
                last.then_inc(S["upd_done"], 1)

            def gates_u(t):
                after(pe, "rank_read", max(t - 1, 0))
                after(pe, "hmt_ready", t)
                rows_by(7, t, G0, 2 * H, "g_done")
                after(pe, "q_ready", t + 1)
                cols_by(turn_a(t), t, U0, "u_done")

            def gate_transposes(t):
                R = ROWS[t]
                after(pe, "gl_ready", t + 1)
                for n in range(2):
                    last = nc.tensor.transpose(B[7][0:H, n * P:n * P + R], glg[0:R, n * H:(n + 1) * H], ident[0:R, 0:R])
                last.then_inc(S["gT_done"], 1)

            def pool_mix(t):
                R = ROWS[t]
                after(pe, "dlt_ready", t + 1)
                after(pe, "dcy_ready", t + 1)
                for n in range(NG):
                    last = mm(bank(0, P, NG, R)[:, n], poolw[:, n, :], dlt[:, n, 0:R])
                last.then_inc(S["pm_done"], 1)

            def out_of_pool(t, i):
                R = ROWS[t]
                after(pe, "mixb_ready", t + 1)
                after(pe, "k_ready", min(i + 1, NT))
                after(pe, "x1_ready", 2 * t)
                after(pe, "wout_in", 16)
                for n, b in enumerate((turn_a(t), turn_b(t))):
                    if n == 1:
                        after(pe, "u_ready", min(i + 1, NT))
                    for k in range(H, KD):
                        mm(B[b][0:R, :], mixT[:, k, 0:R], wout[:, k, 512 * n:512 * n + 512], k == H, False)

            def head_transposes(t):
                R = ROWS[t]
                after(pe, "hm_ready", t + 1)
                after(pe, "nsb_ready", t + 1)
                for h in range(H):
                    last = nc.tensor.transpose(bank(4, P, H, R)[:, h], isb[0:R, h, 0:DH], ident[0:R, 0:R])
                last.then_inc(S["hmt2_done"], 1)

            def out_of_heads(t):
                R = ROWS[t]
                after(pe, "mixa_ready", t + 1)
                for n, (b, name) in enumerate(((turn_a(t), "out0_done"), (turn_b(t), "out_done"))):
                    for k in range(H):
                        last = mm(B[b][0:R, :], mixT[:, k, 0:R], wout[:, k, 512 * n:512 * n + 512], False, k == H - 1)
                    last.then_inc(S[name], 1)

            def router(t):
                R = ROWS[t]
                after(pe, "h2T_ready", t + 1)
                after(pe, "gT_read", min(t + 2, NT))
                after(pe, "rank_read", t)
                after(pe, "hmt_ready", min(t + 1, NT))
                for k in range(KD):
                    last = mm(B[7][0:R, 0:NR], h2T[:, k, 0:R], wr[:, k, :], k == 0, k == KD - 1)
                last.then_inc(S["lo_done"], 1)

            def ranks(t):
                R = ROWS[t]
                after(pe, "route_ready", t + 1)
                after(pe, "hmt_ready", min(t + 2, NT))
                mm(B[7][0:R, 0:NE], ustrict[0:R, 0:R], oh[0:R, t, 2, :])
                mm(B[7][:, NE:2 * NE], ones[0:R, :], oh[0:R, t, 2, :]).then_inc(S["rank_done"], 1)

            after(pe, "ident_ready", 1)
            x_transposes(0)
            for i in range(NT + 2):
                if i < NT:
                    after(pe, "hT_ready", i + 1)
                    after(pe, "k_ready", i)
                    after(pe, "x1_ready", max(2 * i - 3, 0))
                    after(pe, "win_v", 16)
                    rows_by(turn_a(i), i, V0, DM, "v_done")
                if 2 <= i:
                    h2_transposes(i - 2)
                if i < NT:
                    after(pe, "win_o", 16)
                    after(pe, "u_ready", i)
                    after(pe, "x1_ready", 2 * max(i - 1, 0))
                    rows_by(turn_b(i), i, O0, DM, "o_done")
                if 2 <= i:
                    router(i - 2)
                if 1 <= i <= NT:
                    mix_start(i - 1)
                if i < NT:
                    after(pe, "win_q", 16)
                    after(pe, "v_ready", i + 1)
                    cols_by(turn_a(i), i, Q0, "q_done")
                    after(pe, "win_k", 16)
                    after(pe, "eo_ready", i + 1)
                    cols_by(turn_b(i), i, K0, "k_done")
                if i == 0:
                    after(pe, "consts", 1)
                    after(pe, "small_in", 16 * SMALL)
                    for n in range(NG):
                        last = nc.tensor.transpose(bank(5, P, NG, HIST)[:, n], cach[:, n * GW:(n + 1) * GW],
                                                   ident[0:HIST, 0:HIST])
                    last.then_inc(S["hist_done"], 1)
                if 2 <= i:
                    ranks(i - 2)
                if 1 <= i <= NT:
                    pool_mix(i - 1)
                    mix_sums(i - 1)
                if i < NT:
                    after(pe, "win_gu", 16)
                    gates_u(i)
                if 1 <= i <= NT:
                    out_of_pool(i - 1, i)
                    head_transposes(i - 1)
                if i < NT:
                    gate_transposes(i)
                if i + 1 < NT:
                    x_transposes(i + 1)
                if 1 <= i <= NT:
                    out_of_heads(i - 1)
            after(pe, "ul_ready", 2)
            after(pe, "mixa_ready", NT)
            after(pe, "nsb_ready", NT)
            for n in range(2):
                for c in range(NG):
                    last = nc.tensor.transpose(B[4 + n][0:HIST, c * GW:(c + 1) * GW], ulast[:, n, c, :], ident[:, :])
            last.then_inc(S["ulT_done"], 1)

            def gather_transposes(j):
                for n in range(2):
                    pe.wait_ge(gathered[n], 16 * j)
                for (b, k0, k1) in XB:
                    for k in range(k0, k1):
                        for n in range(2):
                            last = nc.tensor.transpose(bank(b, P, k1 - k0, BLOCK)[:, k - k0, n * HALF:(n + 1) * HALF],
                                                       xg[:, n, k * P:(k + 1) * P], ident[0:HALF, 0:HALF])
                    last.then_inc(gx_done, 1)

            after(pe, "ul_out", 1)
            for signal, credit in ((gx_done, 3), (gu_done[0], 2), (gu_done[1], 2), (dn_done, 3), (d0_used, 1), (yb_done, 4)):
                pe.sem_inc(signal, credit)
            gather_transposes(1)
            after(pe, "table_ready", 1)
            nblocks = pe.value_load(tabi[0:1, 2 * (NB + 1):2 * (NB + 1) + 1], min_val=0, max_val=NB)
            with pe.Fori(1, nblocks + 1) as j:
                pe.wait_ge(gx_ready, 3 * j + 3)
                for f in range(KF):
                    if f % 2 == 0:
                        for n in range(2):
                            pe.wait_ge(w_loaded[f + n], 16 * j)
                    pe.wait_ge(hid_ready, 4 * j + max(f - 1, 0))
                    for n, w in enumerate((wg, wu)):
                        for k in range(KD):
                            last = mm(B[2 + f % 2][:, n * BLOCK:(n + 1) * BLOCK], w[:, k, f * P:(f + 1) * P], xgT[:, k, :],
                                      k == 0, k == KD - 1)
                    last.then_inc(gu_done[f // 2], 1)
                pe.wait_ge(y_dve, 2 * j)
                gather_transposes(j + 1)
                pe.wait_ge(hid_ready, 4 * j + 4)
                pe.wait_ge(yT_ready, 3 * j)
                pe.wait_ge(y_act, 2 * j)
                for m in range(KD):
                    if m % 4 == 0:
                        pe.wait_ge(w_loaded[4 + m // 4], 16 * j)
                    n = m // 3
                    for k in range(KF):
                        last = mm(bank(5 + n, P, 3, BLOCK)[:, m % 3], wd[:, k, m * P:(m + 1) * P], hid[:, k, :],
                                  k == 0, k == KF - 1)
                    if m in (2, 5, 7):
                        last.then_inc(dn_done, 1)
                    if m == 3:
                        last.then_inc(d0_used, 1)
                pe.wait_ge(gx_ready, 3 * j + 6)
                for q in YQ:
                    pe.wait_ge(yT_ready, 3 * j + (2 if q % 2 == 0 else 3))
                    for m in range(4):
                        k = 4 * (q % 2) + m
                        last = nc.tensor.transpose(B[YB[q]][0:HALF, m * P:(m + 1) * P],
                                                   yT[:, k, (q // 2) * HALF:(q // 2 + 1) * HALF], ident[:, :])
                    last.then_inc(yb_done, 1)


_INS = ['x_prompt', 'x_sample', 'state_mlstm_C', 'state_mlstm_n', 'state_mlstm_m', 'cache_pool', 'norm1_g', 'w_in',
        'b_gates', 'mh_norm_g', 'pool_w', 'pool_scale', 'w_out', 'norm2_g', 'w_router_group', 'b_router_group',
        'w_router_expert', 'b_router_expert', 'w_gate', 'w_up', 'w_down', 'norm_f_g']


def kernel(**inputs):
    import numpy as _np
    import concourse.bacc as _bacc
    from concourse import mybir as _mybir
    from concourse.bass_utils import run_bass_kernel_spmd as _run

    nc = _bacc.Bacc("TRN2", target_bir_lowering=False, num_devices=1)
    arrays, args = {}, []
    for name in _INS:
        a = _np.ascontiguousarray(inputs[name])
        arrays[f"in_{name}"] = a
        args.append(nc.dram_tensor(f"in_{name}", a.shape, _mybir.dt.from_np(a.dtype), kind="ExternalInput").ap())
    one, seq, d = inputs["x_prompt"].shape
    dec = inputs["x_sample"].shape[1]
    depth, _, h, dh, _ = inputs["state_mlstm_C"].shape
    hist, dp = inputs["cache_pool"].shape[2:]
    state = [(depth, one, h, dh, dh), (depth, one, h, dh), (depth, one, h), (depth, one, hist, dp)]
    shapes = [(one, seq, d), (one, dec, d)] + state + state
    for i, shape in enumerate(shapes):
        args.append(nc.dram_tensor(f"out_{i}", shape, _mybir.dt.float32, kind="ExternalOutput").ap())
    hymba_step(nc, *args)
    r = _run(nc, [arrays], core_ids=[0])
    return tuple(r.results[0][f"out_{i}"] for i in range(len(shapes)))
```
